# Optimizing a Trainium2 kernel written in Bass

```python
import jax, jax.numpy as jnp
from jax import lax
import numpy as np

D_MODEL = 1024
BATCH = 1
SEQ = 512
DEPTH = 2

CHUNK = 64
N_MIXERS = 2
POOL_WINDOWS = (2, 4, 8, 16)
N_POOL_GROUPS = len(POOL_WINDOWS)
POOL_GROUP_DIM = D_MODEL // N_POOL_GROUPS
SGU_BLOCK = 128
SGU_GROUPS = 4
SGU_DIM = D_MODEL
SGU_GROUP_DIM = SGU_DIM // SGU_GROUPS
N_MEM = 256
MEM_HEADS = 4
MEM_HEAD_DIM = D_MODEL // MEM_HEADS
D_FF = 4 * D_MODEL
EPS = 1e-6
N_A_LAYERS = (DEPTH + 1) // 2
N_B_LAYERS = DEPTH // 2

kernel_name = "hybrid_pool_sgu_memory_trunk"

def rmsnorm(x, g):
    xf = x.astype(jnp.float32)
    y = xf * lax.rsqrt(jnp.mean(xf * xf, axis=-1, keepdims=True) + EPS)
    return (y * g.astype(jnp.float32)).astype(x.dtype)

def layernorm(x, g, b):
    xf = x.astype(jnp.float32)
    mu = jnp.mean(xf, axis=-1, keepdims=True)
    var = jnp.mean(jnp.square(xf - mu), axis=-1, keepdims=True)
    y = (xf - mu) * lax.rsqrt(var + EPS)
    return (y * g.astype(jnp.float32) + b.astype(jnp.float32)).astype(x.dtype)

def pool_mixer(h, w_grp, scale):
    B, S, D = h.shape
    hf = h.astype(jnp.float32)
    cs = jnp.pad(jnp.cumsum(hf, axis=1), ((0, 0), (1, 0), (0, 0)))
    csg = cs.reshape(B, S + 1, N_POOL_GROUPS, POOL_GROUP_DIM)
    hg = hf.reshape(B, S, N_POOL_GROUPS, POOL_GROUP_DIM)
    t = jnp.arange(S)
    outs = []
    for g, w in enumerate(POOL_WINDOWS):
        c = csg[:, :, g]
        lo = jnp.maximum(t + 1 - w, 0)
        count = jnp.minimum(t + 1, w).astype(jnp.float32)
        mean = (c[:, t + 1] - c[:, lo]) / count[None, :, None]
        outs.append(mean - hg[:, :, g])
    pooled = jnp.stack(outs, axis=2)
    mixed = jnp.einsum('bsgc,gcd->bsgd', pooled, w_grp.astype(jnp.float32)).reshape(B, S, D)
    return (mixed * scale.astype(jnp.float32)).astype(h.dtype)

def sgu_mask():
    p = jnp.arange(SGU_BLOCK)
    return (p[:, None] // CHUNK) >= (p[None, :] // CHUNK)

def sgu_mixer(h, w_in, ln_g, ln_b, w_s, b_s, w_out):
    B, S, D = h.shape
    z = jax.nn.gelu(h @ w_in)
    u, v = jnp.split(z, 2, axis=-1)
    v = layernorm(v, ln_g, ln_b)
    nblk = S // SGU_BLOCK
    v = v.reshape(B, nblk, SGU_BLOCK, SGU_GROUPS, SGU_GROUP_DIM)
    ws = jnp.where(sgu_mask()[None], w_s, jnp.zeros_like(w_s))
    s = jnp.einsum('gpq,bnqgc->bnpgc', ws, v) + b_s.T[None, None, :, :, None]
    s = s.reshape(B, S, SGU_DIM)
    return (u * s) @ w_out

def mem_attention(h, m, w_q, w_kv, w_o):
    B, S, D = h.shape
    q = (h @ w_q).reshape(B, S, MEM_HEADS, MEM_HEAD_DIM)
    k, v = jnp.split(m @ w_kv, 2, axis=-1)
    k = k.reshape(B, N_MEM, MEM_HEADS, MEM_HEAD_DIM)
    v = v.reshape(B, N_MEM, MEM_HEADS, MEM_HEAD_DIM)
    scores = jnp.einsum('bshd,bnhd->bhsn', q, k).astype(jnp.float32) * (MEM_HEAD_DIM ** -0.5)
    p = jax.nn.softmax(scores, axis=-1).astype(v.dtype)
    o = jnp.einsum('bhsn,bnhd->bshd', p, v).reshape(B, S, D)
    return o @ w_o

def squared_relu_mlp(h, w1, w2):
    return jnp.square(jax.nn.relu(h @ w1)) @ w2

def setup_inputs(seed: int = 0) -> dict:
    key = jax.random.key(seed)
    ks = jax.random.split(key, 24)
    f32 = jnp.float32

    def nrm(k, shape, scale):
        return jax.random.normal(k, shape, f32) * scale

    def gain(k, shape):
        return 1.0 + 0.05 * jax.random.normal(k, shape, f32)

    out_scale = 0.5
    return {
        "x": jax.random.normal(ks[0], (BATCH, SEQ, D_MODEL), f32),
        "mem": jax.random.normal(ks[1], (BATCH, N_MEM, D_MODEL), f32),
        "norm_mix_g": gain(ks[2], (DEPTH, D_MODEL)),
        "norm_mem_g": gain(ks[3], (DEPTH, D_MODEL)),
        "norm_memkv_g": gain(ks[4], (DEPTH, D_MODEL)),
        "norm_ffn_g": gain(ks[5], (DEPTH, D_MODEL)),
        "final_norm_g": gain(ks[6], (D_MODEL,)),
        "pool_w": nrm(ks[7], (N_A_LAYERS, N_POOL_GROUPS, POOL_GROUP_DIM, POOL_GROUP_DIM), POOL_GROUP_DIM ** -0.5),
        "pool_scale": 0.5 + 0.05 * jax.random.normal(ks[8], (N_A_LAYERS, D_MODEL), f32),
        "sgu_w_in": nrm(ks[9], (N_B_LAYERS, D_MODEL, 2 * SGU_DIM), D_MODEL ** -0.5),
        "sgu_ln_g": gain(ks[10], (N_B_LAYERS, SGU_DIM)),
        "sgu_ln_b": nrm(ks[11], (N_B_LAYERS, SGU_DIM), 0.02),
        "sgu_w_s": nrm(ks[12], (N_B_LAYERS, SGU_GROUPS, SGU_BLOCK, SGU_BLOCK), 0.5 * SGU_BLOCK ** -0.5),
        "sgu_b_s": gain(ks[13], (N_B_LAYERS, SGU_GROUPS, SGU_BLOCK)),
        "sgu_w_out": nrm(ks[14], (N_B_LAYERS, SGU_DIM, D_MODEL), out_scale * SGU_DIM ** -0.5),
        "mem_w_q": nrm(ks[15], (DEPTH, D_MODEL, D_MODEL), D_MODEL ** -0.5),
        "mem_w_kv": nrm(ks[16], (DEPTH, D_MODEL, 2 * D_MODEL), D_MODEL ** -0.5),
        "mem_w_o": nrm(ks[17], (DEPTH, D_MODEL, D_MODEL), out_scale * D_MODEL ** -0.5),
        "ffn_w1": nrm(ks[18], (DEPTH, D_MODEL, D_FF), D_MODEL ** -0.5),
        "ffn_w2": nrm(ks[19], (DEPTH, D_FF, D_MODEL), out_scale * D_FF ** -0.5),
    }

def reference(x, mem, norm_mix_g, norm_mem_g, norm_memkv_g, norm_ffn_g, final_norm_g,
              pool_w, pool_scale, sgu_w_in, sgu_ln_g, sgu_ln_b, sgu_w_s, sgu_b_s, sgu_w_out,
              mem_w_q, mem_w_kv, mem_w_o, ffn_w1, ffn_w2):
    for i in range(DEPTH):
        h = rmsnorm(x, norm_mix_g[i])
        j = i // N_MIXERS
        if i % N_MIXERS == 0:
            x = x + pool_mixer(h, pool_w[j], pool_scale[j])
        else:
            x = x + sgu_mixer(h, sgu_w_in[j], sgu_ln_g[j], sgu_ln_b[j],
                              sgu_w_s[j], sgu_b_s[j], sgu_w_out[j])
        h = rmsnorm(x, norm_mem_g[i])
        m = rmsnorm(mem, norm_memkv_g[i])
        x = x + mem_attention(h, m, mem_w_q[i], mem_w_kv[i], mem_w_o[i])
        h = rmsnorm(x, norm_ffn_g[i])
        x = x + squared_relu_mlp(h, ffn_w1[i], ffn_w2[i])
    return rmsnorm(x, final_norm_g)


_drawn_inputs = setup_inputs


def setup_inputs(seed=0):
    import zlib

    import numpy as np

    out = dict(_drawn_inputs(seed))
    spreads = {}
    factors = {'norm_mem_g': 8.0, 'norm_memkv_g': 8.0, 'sgu_ln_g': 8.0, 'sgu_ln_b': 8.0, 'sgu_b_s': 4.402}
    for name, (base, spread) in spreads.items():
        noise = np.random.default_rng([zlib.crc32(name.encode()), seed]).standard_normal(out[name].shape)
        drawn = base * np.exp(spread * noise) if base else spread * noise
        out[name] = __import__('jax').numpy.asarray(drawn.astype(out[name].dtype))
    for name, factor in factors.items():
        out[name] = (out[name] * factor).astype(out[name].dtype)
    return out
```

```python
import numpy as np
import concourse.bass as bass
from concourse import mybir

F32 = mybir.dt.float32
F32R = mybir.dt.float32r
ALU = mybir.AluOpType
ACT = mybir.ActivationFunctionType
AX_X = mybir.AxisListType.X

P = 128
D = 1024
S = 512
NMEM = 256
HEADS = 4
FF = 4096
GROUPS = 4
KT = D // P
ST = S // P
NT = NMEM // P
FB = FF // D
EPS = 1e-6
ATT_SCALE = float(D // HEADS) ** -0.5
WINDOWS = (2, 4, 8, 16)
PAD = 16
RING = 4
AHEAD = RING - 1
BANKS = 8

GAINS = ("mix0", "mix1", "mem0", "mem1", "kv0", "kv1", "ffn0", "ffn1", "final", "pool_scale")

PARTS = (("k0", 8), ("v0", 8), ("pool", 2), ("q0", 8), ("o0", 8), ("f0", 64),
         ("sv", 8), ("su", 8), ("k1", 8), ("v1", 8), ("so", 8), ("q1", 8), ("o1", 8), ("f1", 64))
CHUNKS = sum(n for _, n in PARTS)


def chunk_bases():
    at, base = 0, {}
    for name, n in PARTS:
        base[name] = at
        at += n
    return base


class Numbers:

    def __init__(self):
        self.bank = {}
        self.ready = {}
        self.used = {}
        self.hi = {}
        self.lo = {}
        self.z = {}
        self.count = {"bank": 0, "ready": 0, "hi": 0, "lo": 0, "z": 0}
        self.chunk = chunk_bases()
        self.walk()

    def add(self, key, *kinds):
        maps = {"bank": self.bank, "ready": self.ready, "hi": self.hi, "lo": self.lo, "z": self.z}
        for kind in kinds:
            maps[kind][key] = self.count[kind]
            self.count[kind] += 1

    def tiles(self, name, n, *kinds):
        for i in range(n):
            self.add((name, i), *kinds)

    def projection(self, name, *kinds):
        for m in range(8):
            self.add((name, m), "bank", "ready", *kinds)
            self.used[self.chunk[name] + m] = self.ready[name, m]

    def row_chunk(self, name, i, nt, *kinds):
        if i % 4 < 3:
            self.used[self.chunk[name] + i] = self.count["ready"]
            self.count["ready"] += 1
        else:
            for t in range(nt):
                self.add((name, i // 4 * nt + t), "bank", "ready", *kinds)
            self.used[self.chunk[name] + i] = self.count["ready"] - 1

    def walk(self):
        self.tiles("m0", KT, "hi", "lo")
        self.add("stat_mem", "bank")
        for m in range(8):
            if m == 2:
                self.add("stat_mix0", "bank")
            self.add(("k0", m), "bank", "ready", "z", "hi", "lo")
            self.used[self.chunk["k0"] + m] = self.ready["k0", m]
        for i in range(8):
            self.add(("pooled", i), *(("z", "hi", "lo") if i < 4 else ("hi", "lo")))
            self.row_chunk("v0", i, NT, "hi")
        self.tiles("pool", 8, "bank", "ready")
        for i in range(2):
            self.used[self.chunk["pool"] + i] = self.ready["pool", 4 * i + 3]
        self.attention_and_mlp(0)
        self.add("stat_sgu", "bank")
        for i in range(8):
            self.row_chunk("sv", i, ST)
        self.tiles("ws", 1, "hi", "lo")
        for m in range(8):
            self.add(("su", m), "bank", "ready", "z")
            self.used[self.chunk["su"] + m] = self.ready["su", m]
            if 3 <= m < 7:
                self.add(("v_norm", m - 3), "hi", "lo")
        self.tiles("m1", KT, "hi", "lo")
        self.tiles("sp", 8, "bank", "ready", "z", "hi", "lo")
        self.projection("k1", "z", "hi", "lo")
        for i in range(8):
            self.row_chunk("v1", i, NT, "hi")
        self.projection("so")
        self.attention_and_mlp(1)
        self.add("stat_final", "bank")

    def attention_and_mlp(self, l):
        self.tiles(f"xg_mem{l}", KT, "hi", "lo")
        self.add(f"stat_mem_att{l}", "bank")
        for h in range(HEADS + 2):
            if h < HEADS:
                self.add((f"q{l}", 2 * h), "bank", "ready", "z", "hi", "lo")
            if h >= 2:
                self.tiles(f"pT{l}{h - 2}", 2, "bank", "ready", "hi")
            if h < HEADS:
                self.add((f"q{l}", 2 * h + 1), "bank", "ready", "z", "hi", "lo")
            if 1 <= h <= HEADS:
                self.tiles(f"s{l}{h - 1}", 2, "bank", "ready")
            if h >= 2:
                self.tiles(f"pv{l}{h - 2}", 2, "bank", "ready", "hi")
        for m in range(8):
            self.used[self.chunk[f"q{l}"] + m] = self.ready[f"q{l}", m]
        self.projection(f"o{l}")
        self.tiles(f"xg_ffn{l}", KT, "hi", "lo")
        self.add(f"stat_ffn{l}", "bank")
        for b in range(FB):
            c = self.chunk[f"f{l}"] + 16 * b
            self.tiles(f"fh{l}{b}", 8, "bank", "ready", "z", "hi", "lo")
            self.tiles(f"fo{l}{b}", 8, "bank", "ready")
            for m in range(8):
                self.used[c + m], self.used[c + 8 + m] = self.ready[f"fh{l}{b}", m], self.ready[f"fo{l}{b}", m]
        if l == 0:
            self.tiles("xg_sgu", KT, "hi", "lo")


def trunk_kernel(nc, x_t, mem_t, weights, gains_d, ws_t, bs_d, lng_d, lnb_d, ident_d, corr_d, out):
    C = chunk_bases()
    N = Numbers()
    place = [nc.sbuf_base + (-nc.sbuf_base) % 64]

    def at(offset, name, shape, dt=F32):
        return nc.alloc_sbuf_tensor_at(name, shape, dt, offset=offset)

    def region(nbytes):
        here = place[0]
        place[0] += nbytes + (-nbytes) % 64
        return here

    KB = 1024
    tile_bytes = KT * S * 4
    x = at(region(tile_bytes), "x", [P, KT, S])
    a_off = region(2 * tile_bytes)
    a_hi, a_lo = at(a_off, "a_hi", [P, KT, S], F32R), at(a_off + tile_bytes, "a_lo", [P, KT, S], F32R)
    out_tiles = at(a_off, "out_tiles", [P, KT, S])
    mem_hi, mem_lo = at(a_off, "mem_hi", [P, KT, NMEM], F32R), at(a_off + tile_bytes, "mem_lo", [P, KT, NMEM], F32R)
    b_off = region(2 * tile_bytes)
    b_hi, b_lo = at(b_off, "b_hi", [P, KT, S], F32R), at(b_off + tile_bytes, "b_lo", [P, KT, S], F32R)
    v_raw = at(b_off, "v_raw", [P, ST, D])
    mem_raw = at(b_off + tile_bytes, "mem_raw", [P, KT, NMEM])
    w_raw = at(region(RING * 4 * KB), "w_raw", [P, RING, 1024])
    w_hi = at(region(RING * 4 * KB), "w_hi", [P, RING, 1024], F32R)
    w_lo = at(region(RING * 4 * KB), "w_lo", [P, RING, 1024], F32R)
    kv_off = region(32 * KB)
    k_hi, k_lo = at(kv_off, "k_hi", [P, KT, NMEM], F32R), at(kv_off + 8 * KB, "k_lo", [P, KT, NMEM], F32R)
    v_hi, v_lo = at(kv_off + 16 * KB, "v_hi", [P, NT, D], F32R), at(kv_off + 24 * KB, "v_lo", [P, NT, D], F32R)
    g_hi, g_lo = at(kv_off, "g_hi", [P, ST, D], F32R), at(kv_off + 16 * KB, "g_lo", [P, ST, D], F32R)
    q_off = region(16 * KB)
    q_hi, q_lo = at(q_off, "q_hi", [P, 4, S], F32R), at(q_off + 8 * KB, "q_lo", [P, 4, S], F32R)
    u = at(q_off, "u", [P, KT, S])
    mem_sq = at(q_off, "mem_sq", [P, KT, NMEM])
    pool_buf = at(q_off + 8 * KB, "pool_buf", [P, 3, PAD + S])
    p_off = region(16 * KB)
    probs = at(p_off, "probs", [P, ST, NMEM])
    pt_hi, pt_lo = at(p_off + 8 * KB, "pt_hi", [P, NT, S], F32R), at(p_off + 12 * KB, "pt_lo", [P, NT, S], F32R)
    ln_gain, ln_bias = at(p_off, "ln_gain", [P, D]), at(p_off + 4 * KB, "ln_bias", [P, D])
    ws_raw = at(p_off + 8 * KB, "ws_raw", [P, GROUPS, P])
    ws_hi, ws_lo = at(p_off + 10 * KB, "ws_hi", [P, GROUPS, P], F32R), at(p_off + 12 * KB, "ws_lo", [P, GROUPS, P], F32R)
    bs = at(p_off + 14 * KB, "bs", [P, GROUPS, P])
    x_sq = at(p_off, "x_sq", [P, KT, S])
    pool_h = at(p_off, "pool_h", [P, 4, PAD + S])
    pool_sum = at(p_off + 4 * (PAD + S) * 4, "pool_sum", [P, 2, PAD + S])
    z = at(region(4 * KB), "z", [P, 2, S])
    sq = at(region(4 * KB), "sq", [P, 2, S])
    rstd = at(region(2 * KB), "rstd", [P, S])
    rstd_mem = at(region(KB), "rstd_mem", [P, NMEM])
    ssq = at(region(2 * KB), "ssq", [P, S])
    x2 = at(region(2 * KB), "x2", [P, S])
    diag = at(region(2 * KB), "diag", [P, ST, P])
    ident = at(region(512), "ident", [P, P])
    ones = at(region(512), "ones", [P, P])
    gains = at(region(len(GAINS) * 8 * 4), "gains", [P, len(GAINS) * 8])
    corr = at(region(256), "corr", [P, 4, PAD])
    eps = at(region(64), "eps", [P, 1])
    sd = at(region(64), "sd", [P, ST])
    r_tok = at(region(64), "r_tok", [P, ST])
    mean_sq = at(region(64), "mean_sq", [P, ST])
    root_0 = at(region(64), "root_0", [P, ST])
    root_t = at(region(64), "root_t", [P, ST])
    sd_mem = at(region(64), "sd_mem", [P, NT])
    r_mem = at(region(64), "r_mem", [P, NT])
    row_max = at(region(64), "row_max", [P, ST])
    neg_max = at(region(64), "neg_max", [P, ST])
    row_sum = at(region(64), "row_sum", [P, ST])
    r_sum = at(region(64), "r_sum", [P, ST])
    bn = at(region(ST * 2 * 6 * 4), "bn", [P, ST, 2, 6])
    mv = at(region(64), "mv", [P, ST, 2])
    sd_ln = at(region(64), "sd_ln", [P, ST])
    r_ln = at(region(64), "r_ln", [P, ST])
    assert place[0] <= nc.sbuf_usable_end, (place[0], nc.sbuf_usable_end)

    ps = [nc.alloc_psum_tensor(f"ps{i}", [P, S], F32) for i in range(BANKS)]

    def sem(name):
        return nc.alloc_semaphore(name)

    w_loaded = [sem(f"w_loaded{i}") for i in range(RING)]
    consts_loaded = sem("consts_loaded")
    mem_loaded = [sem(f"mem_loaded{i}") for i in range(3)]
    x_loaded = sem("x_loaded")
    sgu_loaded = sem("sgu_loaded")
    out_stored = sem("out_stored")
    whi_ready = sem("whi_ready")
    wlo_ready = sem("wlo_ready")
    psum_ready = sem("psum_ready")
    taken = sem("taken")
    pooled_ready = sem("pooled_ready")
    hi_ready = sem("hi_ready")
    lo_ready = sem("lo_ready")
    sq_ready = sem("sq_ready")
    squares_ready = sem("squares_ready")
    ssq_step = sem("ssq_step")
    sums_ready = sem("sums_ready")
    sd_ready = sem("sd_ready")
    rtok_ready = sem("rtok_ready")
    root_step = sem("root_step")
    tree_step = sem("tree_step")
    pads_ready = sem("pads_ready")
    gp_step = sem("gp_step")
    gp_pooled = sem("gp_pooled")
    diag_ready = sem("diag_ready")
    bcast_ready = sem("bcast_ready")
    ones_ready = sem("ones_ready")
    pool_step = sem("pool_step")
    max_ready = sem("max_ready")
    negmax_ready = sem("negmax_ready")
    exp_ready = sem("exp_ready")
    rsum_ready = sem("rsum_ready")
    gelu_ready = sem("gelu_ready")
    ln_step = sem("ln_step")
    sdln_ready = sem("sdln_ready")
    norm_ready = sem("norm_ready")
    affine_step = sem("affine_step")
    gated_ready = sem("gated_ready")
    masked = sem("masked")
    out_ready = sem("out_ready")

    def gain(name, m):
        i = GAINS.index(name) * 8 + m
        return gains[:, i:i + 1]

    def bank(key):
        return ps[N.bank[key] % BANKS][:, :]

    with nc.Block() as block:

        @block.sync
        def _(sp):
            def load(c, slot):
                sp.dma_start(w_raw[:, slot, :], weights[c]).then_inc(w_loaded[slot], 16)

            load(0, 0)
            for half in range(2):
                k = slice(KT // 2 * half, KT // 2 * (half + 1))
                sp.dma_start(mem_raw[:, k, :], mem_t[:, k, :]).then_inc(mem_loaded[half], 16)
            load(1, 1)
            sp.dma_start(x[:], x_t).then_inc(x_loaded, 16)
            load(2, 2)
            load(3, 3)
            rounds = CHUNKS // RING
            with sp.Fori(1, rounds) as i:
                for slot in range(RING):
                    sp.wait_ge(wlo_ready, RING * i + slot - RING + 1)
                    load(RING * i + slot, slot)
            for c in range(rounds * RING, CHUNKS):
                sp.wait_ge(wlo_ready, c - RING + 1)
                load(c, c % RING)
            for m in range(KT):
                sp.wait_ge(out_ready, m + 1)
                sp.dma_start(out[m], out_tiles[:, m, :]).then_inc(out_stored, 16)
            sp.wait_ge(out_stored, 16 * KT)

        @block.scalar
        def _(act):
            def hi_weights(c, b=None):
                slot = c % RING
                if b is None:
                    if c >= CHUNKS:
                        return
                    if c >= RING:
                        act.wait_ge(psum_ready, N.used[c - RING] + 1)
                    act.wait_ge(w_loaded[slot], 16 * (c // RING + 1))
                else:
                    act.wait_ge(psum_ready, N.used[c - RING] + 1 + 16 * b)
                    act.wait_ge(w_loaded[slot], 16 * (c // RING + 1) + 64 * b)
                act.activation(w_hi[:, slot, :], w_raw[:, slot, :], ACT.Copy).then_inc(whi_ready, 1)

            def hi(dst, src, scale=1.0):
                act.activation(dst, src, ACT.Copy, scale=scale).then_inc(hi_ready, 1)

            def root(n, src, dst, nt):
                act.wait_ge(sums_ready, n + 1)
                act.activation(dst[:, 0:nt], src[:, 0:nt], ACT.Sqrt, bias=eps[:], scale=1.0 / D).then_inc(sd_ready, 1)

            def hi_residual_tile(xkey, g, m):
                act.wait_ge(taken, N.bank[xkey] + 1)
                hi(a_hi[:, m, :], x[:, m, :], gain(g, m))

            act.dma_start(gains[:], gains_d).then_inc(consts_loaded, 16)
            act.dma_start(ident[:], ident_d).then_inc(consts_loaded, 16)
            act.dma_start(corr[:], corr_d).then_inc(consts_loaded, 16)
            hi_weights(0)
            act.wait_ge(consts_loaded, 48)
            for k in range(KT):
                if k % (KT // 2) == 0:
                    act.wait_ge(mem_loaded[k // (KT // 2)], 16)
                hi(mem_hi[:, k, :], mem_raw[:, k, :], gain("kv0", k))
            act.activation(mem_sq[:], mem_raw[:], ACT.Square).then_inc(squares_ready, 1)
            hi_weights(1)
            hi_weights(2)
            act.wait_ge(ones_ready, 2)
            root(0, bank("stat_mem"), sd_mem, NT)
            act.wait_ge(x_loaded, 16)
            for half in range(2):
                act.activation(x_sq[:, 4 * half:4 * half + 4, :], x[:, 4 * half:4 * half + 4, :],
                               ACT.Square).then_inc(squares_ready, 1)
            for m in range(8):
                if m == 2:
                    root(1, bank("stat_mix0"), sd, ST)
                hi_weights(C["k0"] + m + AHEAD)
                act.wait_ge(taken, N.bank["k0", m] + 1)
                hi(k_hi[:, m, :], z[:, N.z["k0", m] % 2, 0:NMEM])
            for i in range(8):
                hi_weights(C["v0"] + i + AHEAD)
                if i < 4:
                    act.wait_ge(pooled_ready, i + 1)
                    hi(b_hi[:, i, :], z[:, N.z["pooled", i] % 2, :])
                else:
                    act.wait_ge(gp_pooled, i - 3)
                    hi(b_hi[:, i, :], pool_h[:, i - 4, PAD:], gain("mix0", i))
                if i % 4 == 3:
                    for t in range(NT):
                        act.wait_ge(psum_ready, N.ready["v0", i // 4 * 2 + t] + 1)
                        hi(v_hi[:, t, i // 4 * 512:i // 4 * 512 + 512], bank(("v0", i // 4 * 2 + t)), r_mem[:, t:t + 1])
            for m in range(8):
                if m % 4 == 3:
                    hi_weights(C["pool"] + m // 4 + AHEAD)
                hi_residual_tile(("pool", m), "mem0", m)
                act.activation(x_sq[:, m, :], x[:, m, :], ACT.Square).then_inc(squares_ready, 1)

            def attention(l, stat):
                c = C[f"q{l}"]
                root(stat, bank(f"stat_mem_att{l}"), sd, ST)

                def q_tile(m):
                    hi_weights(c + m + AHEAD)
                    act.wait_ge(taken, N.bank[f"q{l}", m] + 1)
                    hi(q_hi[:, m % 4, :], z[:, N.z[f"q{l}", m] % 2, :])

                for h in range(HEADS + 2):
                    if h < HEADS:
                        q_tile(2 * h)
                    if h >= 2:
                        for j in range(NT):
                            act.wait_ge(psum_ready, N.ready[f"pT{l}{h - 2}", j] + 1)
                            hi(pt_hi[:, j, :], bank((f"pT{l}{h - 2}", j)))
                    if h < HEADS:
                        q_tile(2 * h + 1)
                    if 1 <= h <= HEADS:
                        for t in range(ST):
                            act.wait_ge(negmax_ready, 2 * (HEADS * l + h - 1) + t // 2 + 1)
                            act.activation(probs[:, t, :], bank((f"s{l}{h - 1}", t // 2))[:, t % 2 * NMEM:t % 2 * NMEM + NMEM],
                                           ACT.Exp, bias=neg_max[:, t:t + 1], scale=ATT_SCALE,
                                           accum_out=row_sum[:, t:t + 1]).then_inc(exp_ready, 1)
                    if h >= 2:
                        for j in range(2):
                            act.wait_ge(psum_ready, N.ready[f"pv{l}{h - 2}", j] + 1)
                            hi(b_hi[:, 2 * (h - 2) + j, :], bank((f"pv{l}{h - 2}", j)))
                for m in range(8):
                    hi_weights(C[f"o{l}"] + m + AHEAD)
                    hi_residual_tile((f"o{l}", m), f"ffn{l}", m)

            def mlp(l, stat):
                c = C[f"f{l}"]
                root(stat, bank(f"stat_ffn{l}"), sd, ST)
                with act.Fori(0, FB - 1) as b:
                    for m in range(8):
                        hi_weights(c + m + AHEAD, b)
                        act.wait_ge(sq_ready, 8 * FB * l + m + 1 + 8 * b)
                        hi(b_hi[:, m, :], sq[:, m % 2, :])
                    for m in range(8):
                        hi_weights(c + 8 + m + AHEAD, b)
                b = FB - 1
                for m in range(8):
                    hi_weights(c + m + AHEAD + 16 * b)
                    act.wait_ge(sq_ready, 8 * FB * l + m + 1 + 8 * b)
                    hi(b_hi[:, m, :], sq[:, m % 2, :])
                for m in range(8):
                    hi_weights(c + 8 + m + AHEAD + 16 * b)
                    if l == 0:
                        hi_residual_tile((f"fo{l}{b}", m), "mix1", m)
                if l == 1:
                    act.wait_ge(taken, N.bank[f"fo{l}{b}", KT - 1] + 1)
                    act.activation(sq[:, 0, :], x[:, KT - 1, :], ACT.Square).then_inc(squares_ready, 1)

            attention(0, 2)
            act.dma_start(ln_gain[:], lng_d.partition_broadcast(P)).then_inc(sgu_loaded, 16)
            act.dma_start(ln_bias[:], lnb_d.partition_broadcast(P)).then_inc(sgu_loaded, 16)
            act.dma_start(ws_raw[:], ws_t).then_inc(sgu_loaded, 16)
            act.dma_start(bs[:], bs_d.partition_broadcast(P)).then_inc(sgu_loaded, 16)
            mlp(0, 3)

            act.dma_start(mem_raw[:], mem_t).then_inc(mem_loaded[2], 16)
            root(4, bank("stat_sgu"), sd, ST)
            for i in range(8):
                hi_weights(C["sv"] + i + AHEAD)
                if i % 4 == 3:
                    for t in range(ST):
                        r = i // 4 * 4 + t
                        act.wait_ge(psum_ready, N.ready["sv", r] + 1)
                        act.wait_ge(rtok_ready, 5)
                        act.activation(v_raw[:, t, i // 4 * 512:i // 4 * 512 + 512], bank(("sv", r)), ACT.Gelu_apprx_tanh,
                                       scale=r_tok[:, t:t + 1]).then_inc(gelu_ready, 1)
            act.wait_ge(ln_step, ST)
            act.activation(sd_ln[:], mv[:, :, 1], ACT.Sqrt, bias=eps[:]).then_inc(sdln_ready, 1)
            act.wait_ge(masked, 1)
            hi(ws_hi[:], ws_raw[:])
            for m in range(8):
                hi_weights(C["su"] + m + AHEAD)
                act.wait_ge(taken, N.bank["su", m] + 1)
                act.activation(u[:, m, :], z[:, N.z["su", m] % 2, :], ACT.Gelu_apprx_tanh).then_inc(gelu_ready, 1)
                if 3 <= m < 7:
                    act.wait_ge(affine_step, 2 * (m - 3) + 2)
                    hi(g_hi[:, m - 3, :], v_raw[:, m - 3, :])
            act.wait_ge(mem_loaded[2], 16)
            act.wait_ge(psum_ready, N.ready["su", 7] + 1)
            for k in range(KT):
                hi(mem_hi[:, k, :], mem_raw[:, k, :], gain("kv1", k))
            k1_weights_at = (0, 6, 7)
            for m in range(8):
                if m in k1_weights_at:
                    hi_weights(C["k1"] + AHEAD + k1_weights_at.index(m))
                act.wait_ge(gated_ready, m + 1)
                hi(b_hi[:, m, :], sq[:, m % 2, :])
            for m in range(8):
                if m >= 2:
                    hi_weights(C["k1"] + m + RING)
                act.wait_ge(taken, N.bank["k1", m] + 1)
                hi(k_hi[:, m, :], z[:, N.z["k1", m] % 2, 0:NMEM])
            for i in range(8):
                hi_weights(C["v1"] + i + RING)
                if i % 4 == 3:
                    for t in range(NT):
                        act.wait_ge(psum_ready, N.ready["v1", i // 4 * 2 + t] + 1)
                        hi(v_hi[:, t, i // 4 * 512:i // 4 * 512 + 512], bank(("v1", i // 4 * 2 + t)), r_mem[:, t:t + 1])
            for m in range(8):
                if m:
                    hi_weights(C["so"] + m + AHEAD)
                hi_residual_tile(("so", m), "mem1", m)
            attention(1, 5)
            mlp(1, 6)
            root(7, bank("stat_final"), sd, ST)

        @block.vector
        def _(dve):
            def lo_weights(c, slot=None):
                if slot is None:
                    if c >= CHUNKS:
                        return
                    slot = c % RING
                dve.wait_ge(whi_ready, c + 1)
                dve.tensor_tensor(w_lo[:, slot, :], w_raw[:, slot, :], w_hi[:, slot, :].bitcast(F32),
                                  ALU.subtract).then_inc(wlo_ready, 1)

            def lo(n, dst, src, hi_part):
                dve.wait_ge(hi_ready, n + 1)
                return dve.tensor_tensor(dst, src, hi_part.bitcast(F32), ALU.subtract)

            def lo_scaled(n, dst, src, scalar, hi_part):
                dve.wait_ge(hi_ready, n + 1)
                return dve.scalar_tensor_tensor(out=dst, in0=src, scalar=scalar, in1=hi_part.bitcast(F32),
                                                op0=ALU.mult, op1=ALU.subtract)

            def lo_residual(key, g, m):
                lo_scaled(N.hi[key, m], a_lo[:, m, :], x[:, m, :], gain(g, m), a_hi[:, m, :]).then_inc(lo_ready, 1)

            root_steps = [0]

            def reciprocal_root(out_ap, sd_ap, value, nt, ready):
                def step(ins):
                    root_steps[0] += 1
                    ins.then_inc(root_step, 1)
                    dve.wait_ge(root_step, root_steps[0])

                r0, t = root_0[:, 0:nt], root_t[:, 0:nt]
                step(dve.reciprocal(r0, sd_ap))
                step(dve.tensor_tensor(t, r0, r0, ALU.mult))
                step(dve.tensor_tensor(t, t, value, ALU.mult))
                step(dve.tensor_scalar(t, t, -0.5, 1.5, ALU.mult, ALU.add))
                dve.tensor_tensor(out_ap, r0, t, ALU.mult).then_inc(ready, 1)

            def spread(n, key, sd_t, r_t, nt):
                dve.wait_ge(sd_ready, n + 1)
                dve.tensor_scalar(mean_sq[:, 0:nt], bank(key)[:, 0:nt], 1.0 / D, EPS, ALU.mult, ALU.add)
                reciprocal_root(r_t[:, 0:nt], sd_t[:, 0:nt], mean_sq[:, 0:nt], nt, rtok_ready)
                dve.wait_ge(rtok_ready, n + 1)
                for t in range(nt):
                    last = dve.tensor_scalar(diag[:, t, :], ident[:], r_t[:, t:t + 1], None, ALU.mult)
                last.then_inc(diag_ready, 1)
                dst = rstd_mem if nt == NT else rstd
                dve.wait_ge(bcast_ready, n + 1)
                dve.tensor_copy(dst[:], bank(key)[:, 0:nt * P]).then_inc(taken, 1)
                dve.wait_ge(taken, N.bank[key] + 1)

            def normed(key, width=S):
                r = rstd_mem if width == NMEM else rstd
                dve.wait_ge(psum_ready, N.ready[key] + 1)
                dve.tensor_tensor(z[:, N.z[key] % 2, 0:width], bank(key)[:, 0:width], r[:], ALU.mult).then_inc(taken, 1)

            dve.memset(ones[:], 1.0).then_inc(ones_ready, 1)
            dve.memset(eps[:], EPS).then_inc(ones_ready, 1)
            dve.memset(pool_buf[:, :, 0:PAD], 0.0).then_inc(pool_step, 1)
            dve.wait_ge(pool_step, 1)
            lo_weights(0)
            dve.wait_ge(consts_loaded, 48)
            for k in range(KT):
                lo_scaled(N.hi["m0", k], mem_lo[:, k, :], mem_raw[:, k, :], gain("kv0", k), mem_hi[:, k, :]).then_inc(lo_ready, 1)
            trees = [0]

            def add_up(t):
                for n in (4, 2, 1):
                    dve.tensor_tensor(t[:, 0:n, :], t[:, 0:n, :], t[:, n:2 * n, :], ALU.add).then_inc(tree_step, 1)
                    trees[0] += 1
                    dve.wait_ge(tree_step, trees[0])

            dve.wait_ge(squares_ready, 1)
            add_up(mem_sq)
            lo_weights(1)
            lo_weights(2)
            spread(0, "stat_mem", sd_mem, r_mem, NT)
            steps = [1]

            def link(ins):
                steps[0] += 1
                ins.then_inc(pool_step, 1)
                dve.wait_ge(pool_step, steps[0])

            def pooled_tile(t):
                g = t // 2
                h = pool_buf[:, 0, :]
                link(dve.scalar_tensor_tensor(out=h[:, PAD:], in0=x[:, t, :], scalar=gain("mix0", t), in1=rstd[:],
                                              op0=ALU.mult, op1=ALU.mult))
                cur = h
                for level in range(g + 1):
                    nxt = pool_buf[:, 1 + level % 2, :]
                    shift = 1 << level
                    link(dve.tensor_tensor(nxt[:, PAD:], cur[:, PAD:], cur[:, PAD - shift:PAD + S - shift], ALU.add))
                    cur = nxt
                link(dve.tensor_tensor(cur[:, PAD:2 * PAD], cur[:, PAD:2 * PAD], corr[:, g, :], ALU.mult))
                dve.scalar_tensor_tensor(out=z[:, N.z["pooled", t] % 2, :], in0=cur[:, PAD:], scalar=1.0 / WINDOWS[g],
                                         in1=h[:, PAD:], op0=ALU.mult, op1=ALU.subtract).then_inc(pooled_ready, 1)

            for m in range(8):
                if m == 0:
                    dve.wait_ge(squares_ready, 3)
                    add_up(x_sq)
                if m == 2:
                    spread(1, "stat_mix0", sd, r_tok, ST)
                    dve.memset(pool_h[:, :, 0:PAD], 0.0)
                    dve.memset(pool_sum[:, :, 0:PAD], 0.0).then_inc(pads_ready, 1)
                normed(("k0", m), NMEM)
                lo_weights(C["k0"] + m + AHEAD)
                lo(N.hi["k0", m], k_lo[:, m, :], z[:, N.z["k0", m] % 2, 0:NMEM], k_hi[:, m, :]).then_inc(lo_ready, 1)
            for i in range(8):
                if i < 4:
                    pooled_tile(i)
                lo_weights(C["v0"] + i + AHEAD)
                if i < 4:
                    lo(N.hi["pooled", i], b_lo[:, i, :], z[:, N.z["pooled", i] % 2, :], b_hi[:, i, :]).then_inc(lo_ready, 1)
                else:
                    lo_scaled(N.hi["pooled", i], b_lo[:, i, :], pool_h[:, i - 4, PAD:], gain("mix0", i),
                              b_hi[:, i, :]).then_inc(lo_ready, 1)
                if i % 4 == 3:
                    for t in range(NT):
                        key = ("v0", i // 4 * 2 + t)
                        cols = slice(i // 4 * 512, i // 4 * 512 + 512)
                        lo_scaled(N.hi[key], v_lo[:, t, cols], bank(key), r_mem[:, t:t + 1], v_hi[:, t, cols]).then_inc(taken, 1)
            for m in range(8):
                dve.wait_ge(psum_ready, N.ready["pool", m] + 1)
                dve.scalar_tensor_tensor(out=x[:, m, :], in0=bank(("pool", m)), scalar=gain("pool_scale", m), in1=x[:, m, :],
                                         op0=ALU.mult, op1=ALU.add).then_inc(taken, 1)
                if m == 3:
                    lo_weights(C["pool"] + AHEAD)
                if m:
                    lo_residual("xg_mem0", "mem0", m - 1)
            dve.wait_ge(taken, N.bank["pool", 7] + 1)
            lo_residual("xg_mem0", "mem0", 7)
            lo_weights(C["pool"] + 1 + AHEAD)

            def add_residual(key, m):
                dve.wait_ge(psum_ready, N.ready[key, m] + 1)
                dve.tensor_tensor(x[:, m, :], bank((key, m)), x[:, m, :], ALU.add).then_inc(taken, 1)

            def attention(l, stat):
                c = C[f"q{l}"]
                spread(stat, f"stat_mem_att{l}", sd, r_tok, ST)

                def q_tile(m):
                    key = (f"q{l}", m)
                    normed(key)
                    lo_weights(c + m + AHEAD)
                    dve.wait_ge(taken, N.bank[key] + 1)
                    lo(N.hi[key], q_lo[:, m % 4, :], z[:, N.z[key] % 2, :], q_hi[:, m % 4, :]).then_inc(lo_ready, 1)

                def softmax(h):
                    n = HEADS * l + h
                    for j in range(2):
                        key = (f"s{l}{h}", j)
                        dve.wait_ge(psum_ready, N.ready[key] + 1)
                        dve.tensor_reduce(row_max[:, 2 * j:2 * j + 2], bank(key)[:].rearrange("p (t n) -> p t n", t=2),
                                          AX_X, ALU.max).then_inc(max_ready, 1)
                        dve.wait_ge(max_ready, 2 * n + j + 1)
                        dve.tensor_scalar(neg_max[:, 2 * j:2 * j + 2], row_max[:, 2 * j:2 * j + 2], -ATT_SCALE, None,
                                          ALU.mult).then_inc(negmax_ready, 1)
                    dve.wait_ge(exp_ready, ST * (n + 1))
                    dve.reciprocal(r_sum[:], row_sum[:]).then_inc(rsum_ready, 1)
                    dve.wait_ge(rsum_ready, n + 1)
                    for t in range(ST):
                        ins = dve.tensor_scalar(probs[:, t, :], probs[:, t, :], r_sum[:, t:t + 1], None, ALU.mult)
                        if t % 2:
                            ins.then_inc(taken, 1)

                for h in range(HEADS + 2):
                    if h < HEADS:
                        q_tile(2 * h)
                    if h >= 2:
                        for j in range(NT):
                            key = (f"pT{l}{h - 2}", j)
                            lo(N.hi[key], pt_lo[:, j, :], bank(key), pt_hi[:, j, :]).then_inc(taken, 1)
                    if h < HEADS:
                        q_tile(2 * h + 1)
                    if 1 <= h <= HEADS:
                        softmax(h - 1)
                    if h >= 2:
                        for j in range(2):
                            key = (f"pv{l}{h - 2}", j)
                            m = 2 * (h - 2) + j
                            lo(N.hi[key], b_lo[:, m, :], bank(key), b_hi[:, m, :]).then_inc(taken, 1)
                for m in range(8):
                    add_residual(f"o{l}", m)
                    lo_weights(C[f"o{l}"] + m + AHEAD)
                    dve.wait_ge(taken, N.bank[f"o{l}", m] + 1)
                    lo_residual(f"xg_ffn{l}", f"ffn{l}", m)

            def mlp(l, stat):
                c = C[f"f{l}"]
                spread(stat, f"stat_ffn{l}", sd, r_tok, ST)

                def block_of(b, after, split):
                    for m in range(8):
                        key = (f"fh{l}0", m)
                        zt = z[:, N.z[key] % 2, :]
                        dve.wait_ge(psum_ready, N.ready[key] + 1 + 16 * b)
                        dve.tensor_tensor(zt, bank(key), rstd[:], ALU.mult).then_inc(taken, 1)
                        dve.wait_ge(taken, N.bank[key] + 1 + 16 * b)
                        dve.scalar_tensor_tensor(out=sq[:, m % 2, :], in0=zt, scalar=0.0, in1=zt,
                                                 op0=ALU.max, op1=ALU.mult).then_inc(sq_ready, 1)
                        split(m)
                        dve.wait_ge(sq_ready, 8 * FB * l + m + 1 + 8 * b)
                        lo(N.hi[key] + 8 * b, b_lo[:, m, :], sq[:, m % 2, :], b_hi[:, m, :]).then_inc(lo_ready, 1)
                    for m in range(8):
                        key = (f"fo{l}0", m)
                        dve.wait_ge(psum_ready, N.ready[key] + 1 + 16 * b)
                        dve.wait_ge(taken, N.bank[key] - 15 + 16 * b)
                        dve.tensor_tensor(x[:, m, :], bank(key), x[:, m, :], ALU.add).then_inc(taken, 1)
                        split(8 + m)
                        after(m)

                with dve.Fori(0, FB - 1) as b:
                    block_of(b, lambda m: None, lambda j: lo_weights(c + j + AHEAD + 16 * b, (c + j + AHEAD) % RING))
                b = FB - 1

                def next_input(m):
                    dve.wait_ge(taken, N.bank[f"fo{l}{FB - 1}", m] + 1)
                    if l == 0:
                        lo_residual("xg_sgu", "mix1", m)

                block_of(b, next_input, lambda j: lo_weights(c + j + AHEAD + 16 * b))

            attention(0, 2)
            mlp(0, 3)

            spread(4, "stat_sgu", sd, r_tok, ST)
            for i in range(8):
                lo_weights(C["sv"] + i + AHEAD)
                if i % 4 == 3:
                    for t in range(ST):
                        dve.wait_ge(gelu_ready, i // 4 * 4 + t + 1)
                        dve.bn_stats(bn[:, t, i // 4, :], v_raw[:, t, i // 4 * 512:i // 4 * 512 + 512])\
                           .then_inc(taken, 1)
            dve.wait_ge(taken, N.bank['sv', 7] + 1)
            for t in range(ST):
                dve.bn_aggr(mv[:, t, :], bn[:, t, :, :]).then_inc(ln_step, 1)
            dve.wait_ge(sdln_ready, 1)
            dve.tensor_scalar(mean_sq[:], mv[:, :, 1], EPS, None, ALU.add)
            reciprocal_root(r_ln[:], sd_ln[:], mean_sq[:], ST, ln_step)
            dve.wait_ge(ln_step, ST + 1)
            dve.wait_ge(sgu_loaded, 64)
            dve.memset(ws_raw[P // 2:P, :, 0:P // 2], 0.0).then_inc(masked, 1)
            dve.wait_ge(masked, 1)
            lo(N.hi["ws", 0], ws_lo[:], ws_raw[:], ws_hi[:]).then_inc(lo_ready, 1)
            for m in range(8):
                key = ("su", m)
                if m >= 2:
                    dve.wait_ge(gelu_ready, 8 + m - 1)
                normed(key)
                if m < ST:
                    dve.tensor_scalar(v_raw[:, m, :], v_raw[:, m, :], mv[:, m, 0:1], r_ln[:, m:m + 1],
                                      ALU.subtract, ALU.mult).then_inc(norm_ready, 1)
                lo_weights(C["su"] + m + AHEAD)
                if 3 <= m < 7:
                    lo(N.hi["v_norm", m - 3], g_lo[:, m - 3, :], v_raw[:, m - 3, :], g_hi[:, m - 3, :]).then_inc(lo_ready, 1)
            for k in range(KT):
                lo_scaled(N.hi["m1", k], mem_lo[:, k, :], mem_raw[:, k, :], gain("kv1", k), mem_hi[:, k, :]).then_inc(lo_ready, 1)
            dve.wait_ge(gelu_ready, 16)
            k1_weights_at = (1, 7)
            for m in range(8):
                if m in k1_weights_at:
                    lo_weights(C["k1"] + AHEAD + k1_weights_at.index(m))
                key = ("sp", m)
                dve.wait_ge(psum_ready, N.ready[key] + 1)
                dve.tensor_tensor(z[:, N.z[key] % 2, :].rearrange("p (b n) -> p b n", b=ST),
                                  bank(key)[:].rearrange("p (b n) -> p b n", b=ST),
                                  bs[:, m // 2, None, :].broadcast_to([P, ST, P]),
                                  ALU.add).then_inc(taken, 1)
                if m >= 1:
                    lo(N.hi["sp", m - 1], b_lo[:, m - 1, :], sq[:, (m - 1) % 2, :], b_hi[:, m - 1, :]).then_inc(lo_ready, 1)
            lo_weights(C["k1"] + RING + 1)
            lo(N.hi["sp", 7], b_lo[:, 7, :], sq[:, 1, :], b_hi[:, 7, :]).then_inc(lo_ready, 1)
            for m in range(8):
                normed(("k1", m), NMEM)
                if m >= 2:
                    lo_weights(C["k1"] + m + RING)
                lo(N.hi["k1", m], k_lo[:, m, :], z[:, N.z["k1", m] % 2, 0:NMEM], k_hi[:, m, :]).then_inc(lo_ready, 1)
            for i in range(8):
                lo_weights(C["v1"] + i + RING)
                if i % 4 == 3:
                    for t in range(NT):
                        key = ("v1", i // 4 * 2 + t)
                        cols = slice(i // 4 * 512, i // 4 * 512 + 512)
                        lo_scaled(N.hi[key], v_lo[:, t, cols], bank(key), r_mem[:, t:t + 1], v_hi[:, t, cols]).then_inc(taken, 1)
            for m in range(8):
                add_residual("so", m)
                if m:
                    lo_weights(C["so"] + m + AHEAD)
                dve.wait_ge(taken, N.bank["so", m] + 1)
                lo_residual("xg_mem1", "mem1", m)
            attention(1, 5)
            mlp(1, 6)
            spread(7, "stat_final", sd, r_tok, ST)
            for m in range(KT):
                dve.scalar_tensor_tensor(out=out_tiles[:, m, :], in0=x[:, m, :], scalar=gain("final", m), in1=rstd[:],
                                         op0=ALU.mult, op1=ALU.mult).then_inc(out_ready, 1)

        @block.gpsimd
        def _(pool):
            steps = [0]

            def sum_squares(key, tiles=KT):
                for m in range(tiles):
                    pool.wait_ge(taken, N.bank[key, m] + 1)
                    if steps[0]:
                        pool.wait_ge(ssq_step, steps[0])
                    dst = ssq if m == 0 else x2
                    pool.tensor_tensor(dst[:], x[:, m, :], x[:, m, :], ALU.mult).then_inc(ssq_step, 1)
                    steps[0] += 1
                    if m:
                        pool.wait_ge(ssq_step, steps[0])
                        pool.tensor_tensor(ssq[:], ssq[:], x2[:], ALU.add).then_inc(ssq_step, 1)
                        steps[0] += 1

            def gp_link(ins):
                gp_steps[0] += 1
                ins.then_inc(gp_step, 1)
                pool.wait_ge(gp_step, gp_steps[0])

            gp_steps = [0]
            pool.wait_ge(pads_ready, 1)
            pool.wait_ge(x_loaded, 16)
            pool.wait_ge(taken, N.bank["stat_mix0"] + 1)
            for i in range(4):
                g = (4 + i) // 2
                h = pool_h[:, i, :]
                gp_link(pool.tensor_tensor(h[:, PAD:], x[:, 4 + i, :], rstd[:], ALU.mult))
                cur = h
                for level in range(g + 1):
                    nxt = pool_sum[:, level % 2, :]
                    shift = 1 << level
                    gp_link(pool.tensor_tensor(nxt[:, PAD:], cur[:, PAD:], cur[:, PAD - shift:PAD + S - shift], ALU.add))
                    cur = nxt
                gp_link(pool.tensor_tensor(cur[:, PAD:2 * PAD], cur[:, PAD:2 * PAD], corr[:, g, :], ALU.mult))
                gp_link(pool.tensor_scalar(cur[:, PAD:], cur[:, PAD:], 1.0 / WINDOWS[g], 0.0, ALU.mult, ALU.add))
                pool.tensor_tensor(h[:, PAD:], cur[:, PAD:], h[:, PAD:], ALU.subtract).then_inc(gp_pooled, 1)
                pool.wait_ge(gp_pooled, i + 1)
            for m in range(KT):
                pool.wait_ge(squares_ready, 3 + m + 1)
                if m == 0:
                    pool.tensor_copy(ssq[:], x_sq[:, 0, :]).then_inc(ssq_step, 1)
                else:
                    pool.wait_ge(ssq_step, m)
                    pool.tensor_tensor(ssq[:], ssq[:], x_sq[:, m, :], ALU.add).then_inc(ssq_step, 1)
            steps[0] = KT
            sum_squares("o0")
            sum_squares(f"fo0{FB - 1}")
            pool.wait_ge(sgu_loaded, 64)
            for t in range(ST):
                pool.wait_ge(norm_ready, t + 1)
                pool.tensor_tensor(v_raw[:, t, :], v_raw[:, t, :], ln_gain[:], ALU.mult).then_inc(affine_step, 1)
                pool.wait_ge(affine_step, 2 * t + 1)
                pool.tensor_tensor(v_raw[:, t, :], v_raw[:, t, :], ln_bias[:], ALU.add).then_inc(affine_step, 1)
            pool.wait_ge(gelu_ready, 16)
            for m in range(8):
                pool.wait_ge(taken, N.bank["sp", m] + 1)
                if m >= 2:
                    pool.wait_ge(lo_ready, N.lo["sp", m - 2] + 1)
                pool.tensor_tensor(sq[:, m % 2, :], z[:, N.z["sp", m] % 2, :], u[:, m, :], ALU.mult).then_inc(gated_ready, 1)
            sum_squares("so")
            sum_squares("o1")
            sum_squares(f"fo1{FB - 1}", KT - 1)

        @block.tensor
        def _(pe):
            SSQ = 2 * KT - 1

            def three(out_ap, s_hi, s_lo, m_hi, m_lo, start, stop):
                pe.matmul(out_ap, s_hi, m_lo, start=start, stop=False)
                pe.matmul(out_ap, s_hi, m_hi, start=False, stop=False)
                return pe.matmul(out_ap, s_lo, m_hi, start=False, stop=stop)

            def wait_bank(key, step=0):
                if N.bank[key] >= BANKS:
                    pe.wait_ge(taken, N.bank[key] - BANKS + 1 + step)

            def wait_split(key, step=0):
                if key in N.lo:
                    pe.wait_ge(lo_ready, N.lo[key] + 1 + step)
                else:
                    pe.wait_ge(taken, N.bank[key] + 1)

            def ring(c):
                s = c % RING
                return w_hi[:, s, :].rearrange("p (k n) -> p k n", k=KT), w_lo[:, s, :].rearrange("p (k n) -> p k n", k=KT)

            def tile_of(c, key, m_hi, m_lo, need=None, i=0, cstep=0, rstep=0, need_step=0, width=S):
                pe.wait_ge(wlo_ready, c + 1 + cstep)
                wait_bank(key, rstep)
                h, l = ring(c)
                for k in range(KT):
                    if need is not None:
                        wait_split((need, k), need_step)
                    last = three(bank(key)[:, 0:width], h[:, k, :], l[:, k, :], m_hi[:, k, :], m_lo[:, k, :],
                                 k == 0, k == KT - 1)
                last.then_inc(psum_ready, 1)

            def rows_of(name, c0, half, s_hi, s_lo, nt, first_result, need=None):
                for quarter in range(4):
                    c = c0 + 4 * half + quarter
                    pe.wait_ge(wlo_ready, c + 1)
                    h = w_hi[:, c % RING, :].rearrange("p (k n) -> p k n", k=2)
                    l = w_lo[:, c % RING, :].rearrange("p (k n) -> p k n", k=2)
                    for t in range(nt):
                        key = (name, first_result + t)
                        if quarter == 0:
                            wait_bank(key)
                        for j in range(2):
                            k = 2 * quarter + j
                            if need is not None and t == 0:
                                wait_split((need, k))
                            tok = slice(t * P, (t + 1) * P)
                            pe.matmul(bank(key)[:], s_hi[:, k, tok], l[:, j, :], start=(k == 0), stop=False)
                            pe.matmul(bank(key)[:], s_hi[:, k, tok], h[:, j, :], start=False, stop=False)
                            last = pe.matmul(bank(key)[:], s_lo[:, k, tok], h[:, j, :], start=False, stop=(k == KT - 1))
                        if quarter == 3 or t == nt - 1:
                            last.then_inc(psum_ready, 1)
                    yield

            def sums(key, nt, norm=None, squares=None):
                wait_bank(key)
                if squares is None:
                    pe.wait_ge(ssq_step, KT + SSQ * norm)
                for t in range(nt):
                    added = ssq if squares is None else squares[:, 0, :]
                    last = pe.matmul(bank(key)[:, t:t + 1], added[:, t * P:(t + 1) * P], ones[:, 0:1], start=True, stop=True)
                last.then_inc(sums_ready, 1)

            def bcast(n, key, nt):
                pe.wait_ge(diag_ready, n + 1)
                pe.matmul(bank(key)[:, 0:nt * P], ones[:], diag[:, 0:nt, :], start=True, stop=True).then_inc(bcast_ready, 1)

            pe.wait_ge(ones_ready, 1)
            for m in range(8):
                tile_of(C["k0"] + m, ("k0", m), mem_hi, mem_lo, need="m0" if m == 0 else None, width=NMEM)
                if m == 0:
                    pe.wait_ge(tree_step, 3)
                    sums("stat_mem", NT, squares=mem_sq)
                if m == 1:
                    bcast(0, "stat_mem", NT)
                if m == 2:
                    pe.wait_ge(tree_step, 6)
                    sums("stat_mix0", ST, squares=x_sq)
                if m == 3:
                    bcast(1, "stat_mix0", ST)
            for half in range(2):
                for _ in rows_of("v0", C["v0"], half, mem_hi, mem_lo, NT, 2 * half):
                    pass
            for m in range(8):
                g = m // 2
                c = C["pool"] + g // 2
                pe.wait_ge(wlo_ready, c + 1)
                wait_bank(("pool", m))
                for k in range(2):
                    wait_split(("pooled", 2 * g + k))
                    off = (g % 2) * 512 + k * 256 + (m % 2) * P
                    last = three(bank(("pool", m))[:], w_hi[:, c % RING, off:off + P], w_lo[:, c % RING, off:off + P],
                                 b_hi[:, 2 * g + k, :], b_lo[:, 2 * g + k, :], k == 0, k == 1)
                last.then_inc(psum_ready, 1)

            def attention(l, stat, norm):
                c = C[f"q{l}"]

                def q_tile(m):
                    tile_of(c + m, (f"q{l}", m), a_hi, a_lo, need=f"xg_mem{l}" if m == 0 else None)
                    if m == 0:
                        sums(f"stat_mem_att{l}", ST, norm=norm)
                    if m == 1:
                        bcast(stat, f"stat_mem_att{l}", ST)

                def scores(h):
                    wait_split((f"q{l}", 2 * h + 1))
                    for t in range(ST):
                        key = (f"s{l}{h}", t // 2)
                        if t % 2 == 0:
                            wait_bank(key)
                        tok = slice(t * P, (t + 1) * P)
                        for j in range(2):
                            b = (2 * h + j) % 4
                            last = three(bank(key)[:, t % 2 * NMEM:t % 2 * NMEM + NMEM], q_hi[:, b, tok], q_lo[:, b, tok],
                                         k_hi[:, 2 * h + j, :], k_lo[:, 2 * h + j, :], j == 0, j == 1)
                        if t % 2:
                            last.then_inc(psum_ready, 1)

                def transposes(h):
                    for j in range(NT):
                        key = (f"pT{l}{h}", j)
                        wait_bank(key)
                        for t in range(ST):
                            if t % 2 == 0:
                                pe.wait_ge(taken, N.bank[f"s{l}{h}", t // 2] + 1)
                            last = pe.transpose(bank(key)[:, t * P:(t + 1) * P], probs[:, t, j * P:(j + 1) * P], ident[:])
                        last.then_inc(psum_ready, 1)

                def values(h):
                    for j in range(2):
                        key = (f"pv{l}{h}", j)
                        wait_bank(key)
                        cols = slice((2 * h + j) * P, (2 * h + j + 1) * P)
                        for n in range(NT):
                            wait_split((f"pT{l}{h}", n))
                            last = three(bank(key)[:], v_hi[:, n, cols], v_lo[:, n, cols], pt_hi[:, n, :], pt_lo[:, n, :],
                                         n == 0, n == NT - 1)
                        last.then_inc(psum_ready, 1)

                for h in range(HEADS + 2):
                    if h < HEADS:
                        q_tile(2 * h)
                    if h >= 2:
                        transposes(h - 2)
                    if h < HEADS:
                        q_tile(2 * h + 1)
                    if 1 <= h <= HEADS:
                        scores(h - 1)
                    if h >= 2:
                        values(h - 2)
                for m in range(8):
                    c = C[f"o{l}"] + m
                    pe.wait_ge(wlo_ready, c + 1)
                    wait_bank((f"o{l}", m))
                    h, lw = ring(c)
                    for k in range(KT):
                        if m == 0:
                            wait_split((f"pv{l}{k // 2}", k % 2))
                        last = three(bank((f"o{l}", m))[:], h[:, k, :], lw[:, k, :], b_hi[:, k, :], b_lo[:, k, :],
                                     k == 0, k == KT - 1)
                    last.then_inc(psum_ready, 1)

            def mlp(l, stat, norm):
                c = C[f"f{l}"]

                def up(m, b):
                    tile_of(c + m, (f"fh{l}0", m), a_hi, a_lo, need=f"xg_ffn{l}" if m == 0 and isinstance(b, int) and b == 0 else None,
                            cstep=16 * b, rstep=16 * b)

                def down(m, b):
                    tile_of(c + 8 + m, (f"fo{l}0", m), b_hi, b_lo, need=f"fh{l}0" if m == 0 else None,
                            cstep=16 * b, rstep=16 * b, need_step=8 * b)

                up(0, 0)
                sums(f"stat_ffn{l}", ST, norm=norm)
                up(1, 0)
                bcast(stat, f"stat_ffn{l}", ST)
                with pe.Fori(0, FB - 1) as b:
                    for m in range(2, 8):
                        up(m, b)
                    for m in range(8):
                        down(m, b)
                    for m in range(2):
                        up(m, b + 1)
                for m in range(2, 8):
                    up(m, FB - 1)
                for m in range(8):
                    down(m, FB - 1)

            attention(0, 2, 0)
            mlp(0, 3, 1)

            n = 0
            for half in range(2):
                for _ in rows_of("sv", C["sv"], half, a_hi, a_lo, ST, 4 * half, need="xg_sgu" if half == 0 else None):
                    if n == 0:
                        sums("stat_sgu", ST, norm=2)
                    if n == 1:
                        bcast(4, "stat_sgu", ST)
                    n += 1
            for m in range(8):
                tile_of(C["su"] + m, ("su", m), a_hi, a_lo)
            wait_split(("ws", 0))
            for m in range(8):
                wait_bank(("sp", m))
                cols = slice(m * P, (m + 1) * P)
                for b in range(ST):
                    if m == 0:
                        wait_split(("v_norm", b))
                    last = three(bank(("sp", m))[:, b * P:(b + 1) * P], g_hi[:, b, cols], g_lo[:, b, cols],
                                 ws_hi[:, m // 2, :], ws_lo[:, m // 2, :], True, True)
                last.then_inc(psum_ready, 1)
            for m in range(8):
                tile_of(C["k1"] + m, ("k1", m), mem_hi, mem_lo, need="m1" if m == 0 else None, width=NMEM)
            for half in range(2):
                for _ in rows_of("v1", C["v1"], half, mem_hi, mem_lo, NT, 2 * half):
                    pass
            for m in range(8):
                tile_of(C["so"] + m, ("so", m), b_hi, b_lo, need="sp" if m == 0 else None)
            attention(1, 5, 3)
            mlp(1, 6, 4)
            wait_bank("stat_final")
            pe.wait_ge(ssq_step, KT + SSQ * 5 - 2)
            pe.wait_ge(squares_ready, 3 + KT + 1)
            for t in range(ST):
                for i, part in enumerate((ssq, sq[:, 0, :])):
                    last = pe.matmul(bank("stat_final")[:, t:t + 1], part[:, t * P:(t + 1) * P], ones[:, 0:1],
                                     start=(i == 0), stop=(i == 1))
            last.then_inc(sums_ready, 1)
            bcast(7, "stat_final", ST)


def columns(w):
    n = w.shape[1] // P
    return w.reshape(KT, P, n, P).transpose(2, 1, 0, 3).reshape(n, P, KT * P)


def row_pairs(w):
    return w.reshape(4, 2, P, 2, 512).transpose(3, 0, 2, 1, 4).reshape(8, P, 1024)


def kernel(x, mem, norm_mix_g, norm_mem_g, norm_memkv_g, norm_ffn_g, final_norm_g,
           pool_w, pool_scale, sgu_w_in, sgu_ln_g, sgu_ln_b, sgu_w_s, sgu_b_s, sgu_w_out,
           mem_w_q, mem_w_kv, mem_w_o, ffn_w1, ffn_w2):
    import concourse.bacc as bacc
    from concourse.bass_utils import run_bass_kernel_spmd as run

    def channels(a):
        return np.ascontiguousarray(np.asarray(a)[0].T.reshape(KT, P, -1).transpose(1, 0, 2))

    def layer(l):
        w1, w2 = np.asarray(ffn_w1)[l], np.asarray(ffn_w2)[l]
        kv = np.asarray(mem_w_kv)[l]
        ffn = [c for b in range(FB) for c in (columns(w1[:, b * D:(b + 1) * D]), columns(w2[b * D:(b + 1) * D]))]
        return {f"k{l}": columns(kv[:, :D]), f"v{l}": row_pairs(kv[:, D:]), f"q{l}": columns(np.asarray(mem_w_q)[l]),
                f"o{l}": columns(np.asarray(mem_w_o)[l]), f"f{l}": np.concatenate(ffn)}

    parts = {**layer(0), **layer(1)}
    parts["pool"] = np.asarray(pool_w)[0].reshape(2, 2, 2, P, 256).transpose(0, 3, 1, 2, 4).reshape(2, P, 1024)
    w_in = np.asarray(sgu_w_in)[0]
    parts["su"], parts["sv"] = columns(w_in[:, :D]), row_pairs(w_in[:, D:])
    parts["so"] = columns(np.asarray(sgu_w_out)[0])
    weights = np.concatenate([parts[name] for name, _ in PARTS])

    gains = {"mix0": norm_mix_g[0], "mix1": norm_mix_g[1], "mem0": norm_mem_g[0], "mem1": norm_mem_g[1],
             "kv0": norm_memkv_g[0], "kv1": norm_memkv_g[1], "ffn0": norm_ffn_g[0], "ffn1": norm_ffn_g[1],
             "final": final_norm_g, "pool_scale": pool_scale[0]}
    gains = np.concatenate([np.asarray(gains[g]).reshape(KT, P) for g in GAINS])
    count = np.arange(1, PAD + 1)
    corr = np.stack([np.maximum(w / count, 1.0) for w in WINDOWS]).astype(np.float32)
    arrays = {
        "x_t": channels(x), "mem_t": channels(mem), "weights": weights, "gains": np.ascontiguousarray(gains.T),
        "ws_t": np.ascontiguousarray(np.asarray(sgu_w_s)[0].transpose(2, 0, 1)),
        "bs": np.ascontiguousarray(np.asarray(sgu_b_s)[0]),
        "ln_g": np.ascontiguousarray(np.asarray(sgu_ln_g)[0]), "ln_b": np.ascontiguousarray(np.asarray(sgu_ln_b)[0]),
        "ident": np.eye(P, dtype=np.float32), "corr": np.ascontiguousarray(np.broadcast_to(corr, (P, 4, PAD))),
    }
    nc = bacc.Bacc("TRN2", target_bir_lowering=False, num_devices=1, dynamic_dma_scratch_size=8192)
    aps = [nc.dram_tensor(f"in_{name}", a.shape, F32, kind="ExternalInput").ap() for name, a in arrays.items()]
    out = nc.dram_tensor("out_t", (KT, P, S), F32, kind="ExternalOutput").ap()
    trunk_kernel(nc, *aps, out)
    r = run(nc, [{f"in_{name}": a for name, a in arrays.items()}], core_ids=[0])
    out_t = r.results[0]["out_t"]
    return np.ascontiguousarray(out_t.reshape(D, S).T).reshape(1, S, D)
```
